# Optimizing a Trainium2 kernel written in Bass

```python
import jax, jax.numpy as jnp
from jax import lax
import numpy as np

D_MODEL = 1024
BATCH = 1
SEQ = 512
DEPTH = 1

ATTN_HEADS = 8
HEAD_DIM = 64
ATTN_WIDTH = ATTN_HEADS * HEAD_DIM
ROT_DIM = HEAD_DIM // 4
ROPE_THETA = 500000.0
DILATED_PATTERNS = ((128, 1), (512, 4), (2048, 16))
Q_BLOCK = 128
LRU_WIDTH = D_MODEL - ATTN_WIDTH
LRU_BLOCKS = 8
LRU_BLOCK = LRU_WIDTH // LRU_BLOCKS
CONV_WIDTH = 4
LRU_C = 8.0
IN_WIDTH = 3 * ATTN_WIDTH + 2 * LRU_WIDTH
D_FF = 4 * D_MODEL
EPS = 1e-6

kernel_name = "hymba_style_rglru_dilated_attn_block"

def rms_norm(x, g):
    xf = x.astype(jnp.float32)
    y = xf * lax.rsqrt(jnp.mean(xf * xf, axis=-1, keepdims=True) + EPS)
    return (y * g.astype(jnp.float32)).astype(x.dtype)

def partial_rope(x, cos, sin):
    half = ROT_DIM // 2
    xf = x.astype(jnp.float32)
    x1 = xf[..., :half]
    x2 = xf[..., half:ROT_DIM]
    c = cos[None, :, None, :]
    s = sin[None, :, None, :]
    out = jnp.concatenate([x1 * c - x2 * s, x2 * c + x1 * s, xf[..., ROT_DIM:]], axis=-1)
    return out.astype(x.dtype)

def dilated_attention(q, k, v):
    B, S, H, Dh = q.shape
    scale = HEAD_DIM ** -0.5
    n_blocks = S // Q_BLOCK

    def one_block(start):
        qb = lax.dynamic_slice_in_dim(q, start, Q_BLOCK, axis=1)
        t = start + jnp.arange(Q_BLOCK)
        outs, lses = [], []
        for w, d in DILATED_PATTERNS:
            offs = jnp.arange(w // d + 1) * d
            idx = t[:, None] - offs[None, :]
            valid = idx >= 0
            idx = jnp.maximum(idx, 0)
            kg = jnp.take(k, idx, axis=1)
            vg = jnp.take(v, idx, axis=1)
            s = jnp.einsum('bqhd,bqnhd->bhqn', qb, kg,
                           preferred_element_type=jnp.float32) * scale
            s = jnp.where(valid[None, None], s, -jnp.inf)
            lse = jax.nn.logsumexp(s, axis=-1)
            p = jnp.exp(s - lse[..., None])
            o = jnp.einsum('bhqn,bqnhd->bqhd', p, vg.astype(jnp.float32))
            outs.append(o)
            lses.append(lse)
        alpha = jax.nn.softmax(jnp.stack(lses, axis=0), axis=0)
        alpha = jnp.transpose(alpha, (0, 1, 3, 2))[..., None]
        out = jnp.sum(alpha * jnp.stack(outs, axis=0), axis=0)
        return out.astype(q.dtype)

    starts = jnp.arange(n_blocks) * Q_BLOCK
    blocks = lax.map(one_block, starts)
    return jnp.transpose(blocks, (1, 0, 2, 3, 4)).reshape(B, S, H, Dh)

def _lin_comb(left, right):
    a1, b1 = left
    a2, b2 = right
    return a1 * a2, a2 * b1 + b2

def rg_lru_branch(xb, gate_in, conv_w, conv_b, w_r, b_r, w_i, b_i, lam):
    B, S, _ = xb.shape
    xp = jnp.pad(xb, ((0, 0), (CONV_WIDTH - 1, 0), (0, 0)))
    xc = conv_b + sum(xp[:, j:j + S] * conv_w[j] for j in range(CONV_WIDTH))
    xf = xc.astype(jnp.float32)
    xblk = xf.reshape(B, S, LRU_BLOCKS, LRU_BLOCK)
    r = jax.nn.sigmoid(jnp.einsum('bsnc,ncd->bsnd', xblk, w_r.astype(jnp.float32))
                       + b_r.astype(jnp.float32)).reshape(B, S, LRU_WIDTH)
    i = jax.nn.sigmoid(jnp.einsum('bsnc,ncd->bsnd', xblk, w_i.astype(jnp.float32))
                       + b_i.astype(jnp.float32)).reshape(B, S, LRU_WIDTH)
    log_a = -LRU_C * r * jax.nn.softplus(-lam.astype(jnp.float32))
    a = jnp.exp(log_a)
    bx = jnp.sqrt(-jnp.expm1(2.0 * log_a)) * (i * xf)
    _, h = lax.associative_scan(_lin_comb, (a, bx), axis=1)
    y = jax.nn.gelu(gate_in.astype(jnp.float32)) * h
    return y.astype(xb.dtype)

def setup_inputs(seed: int = 0) -> dict:
    key = jax.random.key(seed)
    ks = jax.random.split(key, 20)
    f32 = jnp.float32
    nrm = lambda k, shape, scale: jax.random.normal(k, shape, f32) * scale
    gain = lambda k, shape: 1.0 + 0.02 * jax.random.normal(k, shape, f32)
    x = jax.random.normal(ks[0], (BATCH, SEQ, D_MODEL), f32)
    u = jax.random.uniform(ks[9], (DEPTH, LRU_WIDTH), f32, 0.9, 0.999)
    a0 = u ** (1.0 / LRU_C)
    lru_lambda = jnp.log(a0) - jnp.log1p(-a0)
    return {
        "x": x,
        "norm1_g": gain(ks[1], (DEPTH, D_MODEL)),
        "w_in": nrm(ks[2], (DEPTH, D_MODEL, IN_WIDTH), D_MODEL ** -0.5),
        "conv_w": nrm(ks[3], (DEPTH, CONV_WIDTH, LRU_WIDTH), CONV_WIDTH ** -0.5),
        "conv_b": nrm(ks[4], (DEPTH, LRU_WIDTH), 0.02),
        "w_rgate": nrm(ks[5], (DEPTH, LRU_BLOCKS, LRU_BLOCK, LRU_BLOCK), LRU_BLOCK ** -0.5),
        "b_rgate": nrm(ks[6], (DEPTH, LRU_BLOCKS, LRU_BLOCK), 0.02),
        "w_igate": nrm(ks[7], (DEPTH, LRU_BLOCKS, LRU_BLOCK, LRU_BLOCK), LRU_BLOCK ** -0.5),
        "b_igate": nrm(ks[8], (DEPTH, LRU_BLOCKS, LRU_BLOCK), 0.02),
        "lru_lambda": lru_lambda,
        "attn_out_g": gain(ks[10], (DEPTH, ATTN_WIDTH)),
        "lru_out_g": gain(ks[11], (DEPTH, LRU_WIDTH)),
        "w_out": nrm(ks[12], (DEPTH, D_MODEL, D_MODEL), D_MODEL ** -0.5),
        "norm2_g": gain(ks[13], (DEPTH, D_MODEL)),
        "w_mlp_up": nrm(ks[14], (DEPTH, D_MODEL, D_FF), D_MODEL ** -0.5),
        "w_mlp_down": nrm(ks[15], (DEPTH, D_FF, D_MODEL), D_FF ** -0.5),
        "final_g": gain(ks[16], (D_MODEL,)),
    }

def reference(x, norm1_g, w_in, conv_w, conv_b, w_rgate, b_rgate, w_igate, b_igate,
              lru_lambda, attn_out_g, lru_out_g, w_out, norm2_g, w_mlp_up, w_mlp_down,
              final_g):
    B, S, _ = x.shape
    pos = jnp.arange(S, dtype=jnp.float32)
    inv_freq = ROPE_THETA ** (-jnp.arange(0, ROT_DIM, 2, dtype=jnp.float32) / ROT_DIM)
    ang = pos[:, None] * inv_freq[None, :]
    cos, sin = jnp.cos(ang), jnp.sin(ang)
    splits = [ATTN_WIDTH, 2 * ATTN_WIDTH, 3 * ATTN_WIDTH, 3 * ATTN_WIDTH + LRU_WIDTH]
    h = x
    for l in range(DEPTH):
        u = rms_norm(h, norm1_g[l])
        z = u @ w_in[l]
        q, k, v, xl, gl = jnp.split(z, splits, axis=-1)
        q = partial_rope(q.reshape(B, S, ATTN_HEADS, HEAD_DIM), cos, sin)
        k = partial_rope(k.reshape(B, S, ATTN_HEADS, HEAD_DIM), cos, sin)
        v = v.reshape(B, S, ATTN_HEADS, HEAD_DIM)
        attn = dilated_attention(q, k, v).reshape(B, S, ATTN_WIDTH)
        lru = rg_lru_branch(xl, gl, conv_w[l], conv_b[l], w_rgate[l], b_rgate[l],
                            w_igate[l], b_igate[l], lru_lambda[l])
        mixed = jnp.concatenate([rms_norm(attn, attn_out_g[l]),
                                 rms_norm(lru, lru_out_g[l])], axis=-1)
        h = h + mixed @ w_out[l]
        u = rms_norm(h, norm2_g[l])
        f = jnp.square(jax.nn.relu(u @ w_mlp_up[l]))
        h = h + f @ w_mlp_down[l]
    return rms_norm(h, final_g)


_drawn_inputs = setup_inputs


def setup_inputs(seed=0):
    import zlib

    import numpy as np

    out = dict(_drawn_inputs(seed))
    spreads = {}
    factors = {'b_rgate': 8.0,
     'b_igate': 8.0,
     'attn_out_g': 5.121,
     'lru_out_g': 5.056,
     'norm2_g': 3.597,
     'final_g': 2.856}
    for name, (base, spread) in spreads.items():
        noise = np.random.default_rng([zlib.crc32(name.encode()), seed]).standard_normal(out[name].shape)
        drawn = base * np.exp(spread * noise) if base else spread * noise
        out[name] = __import__('jax').numpy.asarray(drawn.astype(out[name].dtype))
    for name, factor in factors.items():
        out[name] = (out[name] * factor).astype(out[name].dtype)
    return out
```

```python
import concourse.bass as bass
from concourse import mybir
from contextlib import ExitStack

SEQ, D_MODEL, D_FF = 512, 1024, 4096
HEADS, HEAD_DIM, ROT = 8, 64, 16
WIDTH = HEADS * HEAD_DIM
CONV_WIDTH = 4
EPS = 1e-6
P = 128
COLS = 512
TILES = SEQ // P
KB = D_MODEL // P
CB = WIDTH // P
UNIT_KB = 2
PANEL_UNITS = KB // UNIT_KB
RAW = 4
RING = 6
MLP_RING = 8
GROUP_FF = 1024
GROUPS = D_FF // GROUP_FF
PARAM_ROWS = CONV_WIDTH * CB + 5 * CB
LAG = 2
MASKED = -1e30
IN_PANELS = [("q", 0), ("xl", 3), ("gl", 4), ("k", 1), ("v", 2)]
IN_UNITS = PANEL_UNITS * len(IN_PANELS)
IN_STEPS = TILES * len(IN_PANELS)
OUT_UNITS = 2 * PANEL_UNITS
MIX_UNITS = IN_UNITS + OUT_UNITS
GROUP_UNITS = 4 * PANEL_UNITS
GROUP_STEPS = 8
ITEMS = HEADS * TILES
BANKS = 4


def layer_kernel(nc, x, norm1_g, w_in, conv_w, conv_b, w_rgate, b_rgate, w_igate, b_igate, lru_lambda,
                 attn_out_g, lru_out_g, w_out, norm2_g, w_mlp_up, w_mlp_down, final_g,
                 pattern_bias, rope_table, out):
    f32, f32r = mybir.dt.float32, mybir.dt.float32r
    ALU, ACT, AX = mybir.AluOpType, mybir.ActivationFunctionType, mybir.AxisListType

    w_in_v = w_in[0].rearrange("(kb p) c -> p kb c", p=P)
    w_out_v = w_out[0].rearrange("(kb p) c -> p kb c", p=P)
    w_up_v = w_mlp_up[0].rearrange("(kb p) c -> p kb c", p=P)
    w_down_v = w_mlp_down[0].rearrange("(kb p) c -> p kb c", p=P)

    ctx = ExitStack()
    with ctx:
        def sb(name, shape, dt=f32, stack=ctx):
            return stack.enter_context(nc.sbuf_tensor(name, shape, dt))

        def sem(name):
            return ctx.enter_context(nc.semaphore(name))

        raw = sb("raw", [P, RAW, UNIT_KB, COLS])
        w_hi = [sb(f"w_hi{s}", [P, UNIT_KB, COLS], f32r) for s in range(RING)]
        w_lo = [sb(f"w_lo{s}", [P, UNIT_KB, COLS], f32r) for s in range(RING)]
        u_hi = sb("u_hi", [P, KB, SEQ], f32r)
        u_lo = sb("u_lo", [P, KB, SEQ], f32r)
        xs = sb("xs", [P, TILES, D_MODEL])
        gain = sb("gain", [P, D_MODEL])
        attn_gain = sb("attn_gain", [P, WIDTH])
        ident = sb("ident", [P, P])
        ones = sb("ones", [P, 1])
        minus_half = sb("minus_half", [P, TILES])
        bias8 = sb("bias8", [P, SEQ])
        rope = sb("rope", [P, TILES, 2 * ROT])
        rope_tmp = sb("rope_tmp", [P, 2, HEADS, ROT])
        prob = sb("prob", [P, 3, SEQ])
        prob_t = sb("prob_t", [P, 2, SEQ])
        param_rows = sb("param_rows", [PARAM_ROWS, P])
        params = sb("params", [P, PARAM_ROWS])
        small = sb("small", [P, 8, CB])
        decay = sb("decay", [P, 2, CB])
        sum_sq = sb("sum_sq", [P, 4, 2 * TILES])
        mean_sq = sb("mean_sq", [P, 5, TILES])
        rstd = sb("rstd", [P, 5, TILES])
        lru_sq = sb("lru_sq", [P, TILES])
        neg_max = sb("neg_max", [P, ITEMS])
        denom = sb("denom", [P, ITEMS])
        inv_denom = sb("inv_denom", [P, ITEMS])
        N1, ATT, N2, FIN, LRU = range(5)

        mixer = ExitStack()
        first = ExitStack()
        gate_in = sb("gate_in", [P, CB, SEQ], stack=first)
        decay_a = sb("decay_a", [P, CB, SEQ], stack=first)
        gelu_g = sb("gelu_g", [P, CB, SEQ], stack=first)
        conv_in = sb("conv_in", [P, CB, SEQ + CONV_WIDTH - 1], stack=first)
        first.close()
        lru_hi = sb("lru_hi", [P, CB, SEQ], f32r, stack=mixer)
        lru_lo = sb("lru_lo", [P, CB, SEQ], f32r, stack=mixer)
        att_hi = sb("att_hi", [P, CB, SEQ], f32r, stack=mixer)
        att_lo = sb("att_lo", [P, CB, SEQ + CONV_WIDTH - 1], f32r, stack=mixer)
        hidden = sb("hidden", [P, CB, SEQ], stack=mixer)
        gate_r = sb("gate_r", [P, CB, SEQ], stack=mixer)
        qT = sb("qT", [P, CB, SEQ], stack=mixer)
        kT = sb("kT", [P, CB, SEQ], stack=mixer)
        att = sb("att", [P, 2, WIDTH], stack=mixer)
        mixer.close()
        mlp = ExitStack()
        f_hi = sb("f_hi", [P, KB, SEQ], f32r, stack=mlp)
        f_lo = sb("f_lo", [P, KB, SEQ], f32r, stack=mlp)
        sb("tail_of_att_lo", [P, CB * (CONV_WIDTH - 1) + 4], stack=mlp)
        w_hi += [sb(f"w_hi{s}", [P, UNIT_KB, COLS], f32r, stack=mlp) for s in range(RING, MLP_RING)]
        w_lo += [sb(f"w_lo{s}", [P, UNIT_KB, COLS], f32r, stack=mlp) for s in range(RING, MLP_RING)]
        normed = sb("normed", [P, 2, D_MODEL], stack=mlp)
        final_gain = sb("final_gain", [P, D_MODEL], stack=mlp)
        relu = sb("relu", [P, 2, SEQ], stack=mlp)
        f_full = sb("f_full", [P, 2, SEQ], stack=mlp)
        ctx.enter_context(mlp)
        values = gate_r
        normed1 = hidden[:, :, :].rearrange("p (b a) s -> p b (a s)", b=2)
        gate_w = prob_t[:, :, :].rearrange("p g (c d) -> p g c d", d=P)

        ps = [ctx.enter_context(nc.psum_tensor(f"ps{2 * n}{2 * n + 1}", [P, 2 * COLS], f32)) for n in range(4)]

        def bank(b, cols=COLS):
            return ps[b // 2][:, (b % 2) * COLS:(b % 2) * COLS + cols]

        x_in = [sem(f"x_in{t}") for t in range(TILES)]
        raw_in = [sem(f"raw_in{s}") for s in range(RAW)]
        gain1_in, gain2_in, final_gain_in = sem("gain1_in"), sem("gain2_in"), sem("final_gain_in")
        tables_in, param_in, gate_w_in = sem("tables_in"), sem("param_in"), sem("gate_w_in")
        out_stored = [sem(f"out_stored{b}") for b in range(2)]
        pool_step, consts_ready, gate_w_clear = sem("pool_step"), sem("consts_ready"), sem("gate_w_clear")
        hi_done, lo_done, unit_used = sem("hi_done"), sem("lo_done"), sem("unit_used")
        step_done, in_evac, out_evac = sem("step_done"), sem("in_evac"), sem("out_evac")
        sq_done, rstd_ready = sem("sq_done"), sem("rstd_ready")
        row_normed, rows_turned = sem("row_normed"), sem("rows_turned")
        u_hi_done, u_ready = sem("u_hi_done"), sem("u_ready")
        dve_step, params_turned, params_ready, decay_ready = sem("dve_step"), sem("params_turned"), sem("params_ready"), sem("decay_ready")
        exp_lam = sem("exp_lam")
        roped, qk_turned, qk_evac = sem("roped"), sem("qk_turned"), sem("qk_evac")
        conv_done, gates_done, sig_done = sem("conv_done"), sem("gates_done"), sem("sig_done")
        a_done, tanh_done, a_sq_done, ix_done = sem("a_done"), sem("tanh_done"), sem("a_sq_done"), sem("ix_done")
        root_arg, root_done, y_done = sem("root_arg"), sem("root_done"), sem("y_done")
        y_sq_done, y_sq_added, lru_hi_done, lru_ready = sem("y_sq_done"), sem("y_sq_added"), sem("lru_hi_done"), sem("lru_ready")
        lru_sum_done, lru_sum_read, lru_rstd = sem("lru_sum_done"), sem("lru_sum_read"), sem("lru_rstd")
        scores_done, max_done, exp_done = sem("scores_done"), sem("max_done"), sem("exp_done")
        prob_turned, even_evac, odd_evac, pv_done = sem("prob_turned"), sem("even_evac"), sem("odd_evac"), sem("pv_done")
        att_out, att_sq, att_gained, att_turned = sem("att_out"), sem("att_sq"), sem("att_gained"), sem("att_turned")
        att_hi_done, att_ready, att_rstd = sem("att_hi_done"), sem("att_ready"), sem("att_rstd")
        sq2_done, rstd2_ready, row2_normed, rows2_turned = sem("sq2_done"), sem("rstd2_ready"), sem("row2_normed"), sem("rows2_turned")
        u2_hi_done, u2_ready = sem("u2_hi_done"), sem("u2_ready")
        up_done, up_free, down_done, down_free = sem("up_done"), sem("up_free"), sem("down_done"), sem("down_free")
        relu_done, squared, f_hi_done, f_ready = sem("relu_done"), sem("squared"), sem("f_hi_done"), sem("f_ready")
        mlp_unit_used = sem("mlp_unit_used")
        sq3_done, rstd3_ready, final_normed = sem("sq3_done"), sem("rstd3_ready"), sem("final_normed")

        def slot_of(n):
            if n < MIX_UNITS:
                return n % RING
            m = (n - MIX_UNITS) % MLP_RING
            return RING + m if m < 2 else (MIX_UNITS + m - MLP_RING) % RING

        def wait_unit_released(eng, n):
            if n < IN_UNITS:
                panel, q = divmod(n, PANEL_UNITS)
                if q == PANEL_UNITS - 1:
                    eng.wait_ge(step_done, TILES * (panel + 1))
                else:
                    eng.wait_ge(unit_used, (PANEL_UNITS - 1) * panel + q + 1)
                return
            used = (PANEL_UNITS - 1) * len(IN_PANELS)
            half, q = divmod(n - IN_UNITS, 2)
            if q == 0:
                eng.wait_ge(unit_used, used + half + 1)
            else:
                eng.wait_ge(step_done, IN_STEPS + (4, 8, 15, 16)[half])

        def wait_split_slot(eng, n):
            if n < MIX_UNITS:
                if n >= RING:
                    wait_unit_released(eng, n - RING)
            elif n < MIX_UNITS + 2:
                eng.wait_ge(pv_done, ITEMS)
            elif n < MIX_UNITS + MLP_RING:
                wait_unit_released(eng, n - MLP_RING)

        def wait_mlp_slot(eng, i, j, q):
            i, j = (i, j - 2) if j >= 2 else (i - 1, j + 2)
            if q < PANEL_UNITS - 1:
                eng.wait_ge(mlp_unit_used, 12 * i + 3 * j + q + 1)
            elif j < 2:
                eng.wait_ge(up_done, 8 * i + 4 * j + 4)
            else:
                eng.wait_ge(down_done, 8 * i + 4 * (j - 2) + 4)

        block = ctx.enter_context(nc.Block())

        @block.sync
        def _(sp):
            def load_x(t):
                sp.dma_start(xs[:, t, :], x[0, t * P:(t + 1) * P, :]).then_inc(x_in[t], 16)

            def load_unit(n, src):
                if n >= RAW:
                    sp.wait_ge(lo_done, n - RAW + 1)
                sp.dma_start(raw[:, n % RAW, :, :], src).then_inc(raw_in[n % RAW], 16)

            def in_unit(n):
                panel, q = divmod(n, PANEL_UNITS)
                c = IN_PANELS[panel][1] * COLS
                load_unit(n, w_in_v[:, UNIT_KB * q:UNIT_KB * (q + 1), c:c + COLS])

            load_x(0)
            in_unit(0)
            in_unit(1)
            load_x(1)
            in_unit(2)
            in_unit(3)
            load_x(2)
            load_x(3)
            row = 0
            for src in (conv_w[0].rearrange("j (c p) -> (j c) p", p=P), conv_b.rearrange("a (c p) -> (a c) p", p=P),
                        lru_lambda.rearrange("a (c p) -> (a c) p", p=P),
                        b_rgate[0].rearrange("(c e) d -> c e d", e=2), b_igate[0].rearrange("(c e) d -> c e d", e=2),
                        lru_out_g.rearrange("a (c p) -> (a c) p", p=P)):
                n = CONV_WIDTH * CB if row == 0 else CB
                dst = param_rows[row:row + n, :]
                if len(src.shape) == 3:
                    dst = dst.rearrange("c (e d) -> c e d", e=2)
                sp.dma_start(dst, src).then_inc(param_in, 16)
                row += n
            for n in range(4, IN_UNITS):
                in_unit(n)
                if n == PANEL_UNITS + 2:
                    sp.wait_ge(row_normed, TILES)
                    sp.dma_start(gain[:, :], norm2_g[0:1, :].to_broadcast([P, D_MODEL])).then_inc(gain2_in, 16)
            for half in range(4):
                rows, hf = divmod(half, 2)
                for q in range(2):
                    kb = CB * (1 - rows) + UNIT_KB * q
                    load_unit(IN_UNITS + 2 * half + q, w_out_v[:, kb:kb + UNIT_KB, hf * COLS:(hf + 1) * COLS])

            def group_unit(i, j, q):
                n = GROUP_UNITS * i + MIX_UNITS + PANEL_UNITS * j + q
                sp.wait_ge(lo_done, n - RAW + 1)
                if j < 2:
                    src = w_up_v[:, UNIT_KB * q:UNIT_KB * (q + 1), bass.ds(i * GROUP_FF + j * COLS, COLS)]
                else:
                    src = w_down_v[:, bass.ds(i * KB + UNIT_KB * q, UNIT_KB), (j - 2) * COLS:(j - 1) * COLS]
                sp.dma_start(raw[:, (MIX_UNITS + PANEL_UNITS * j + q) % RAW, :, :], src)\
                  .then_inc(raw_in[(MIX_UNITS + PANEL_UNITS * j + q) % RAW], 16)

            with sp.Fori(0, GROUPS) as i:
                for j in range(4):
                    for q in range(PANEL_UNITS):
                        group_unit(i, j, q)
            sp.dma_start(final_gain[:, :], final_g.rearrange("(a n) -> a n", a=1).to_broadcast([P, D_MODEL]))\
              .then_inc(final_gain_in, 16)
            for t in range(TILES):
                sp.wait_ge(final_normed, t + 1)
                sp.dma_start(out[0, t * P:(t + 1) * P, :], normed[:, t % 2, :]).then_inc(out_stored[t % 2], 16)
            for b in range(2):
                sp.wait_ge(out_stored[b], 16 * TILES // 2)

        @block.gpsimd
        def _(pool):
            steps = [0]

            def then(ins):
                steps[0] += 1
                ins.then_inc(pool_step, 1)
                pool.wait_ge(pool_step, steps[0])

            then(pool.memset(ident[:, :], 0.0))
            then(pool.affine_select(out=ident[:, :], in_=ident[:, :], compare_op=ALU.not_equal, fill=1.0, base=0,
                                    pattern=[[-1, P]], channel_multiplier=1))
            then(pool.memset(ones[:, :], 1.0))
            then(pool.memset(minus_half[:, :], -0.5))
            then(pool.memset(prob_t[:, :, :], 0.0))
            pool.memset(conv_in[:, :, 0:CONV_WIDTH - 1], 0.0).then_inc(consts_ready, 1)

            def inverse_rms(kind, t, n, total, done):
                width = D_MODEL if kind in (N1, N2, FIN) else WIDTH
                then(pool.tensor_scalar(mean_sq[:, kind, t:t + n], total, 1.0 / width, EPS, ALU.mult, ALU.add))
                pool.tensor_tensor(rstd[:, kind, t:t + n], mean_sq[:, kind, t:t + n], minus_half[:, 0:n], ALU.pow)\
                    .then_inc(done, 1)

            def add_halves(kind, t):
                then(pool.tensor_tensor(sum_sq[:, kind, t:t + 1], sum_sq[:, kind, t:t + 1],
                                        sum_sq[:, kind, TILES + t:TILES + t + 1], ALU.add))

            def rope_tile(r):
                t = r % TILES
                z = prob[:, r % 3, :].rearrange("p (h d) -> p h d", d=HEAD_DIM)
                half = ROT // 2
                cos = rope[:, t:t + 1, 0:ROT].to_broadcast([P, HEADS, ROT])
                sin = rope[:, t:t + 1, ROT:ROT + half].to_broadcast([P, HEADS, half])
                pool.wait_ge(in_evac, r + 1 if r < TILES else 2 * TILES + r + 1)
                if r == 0:
                    pool.wait_ge(tables_in, 48)
                pool.tensor_tensor(rope_tmp[:, 0, :, :], z[:, :, 0:ROT], cos, ALU.mult)
                pool.tensor_tensor(rope_tmp[:, 1, :, 0:half], z[:, :, half:ROT], sin, ALU.mult)
                then(pool.tensor_tensor(rope_tmp[:, 1, :, half:ROT], z[:, :, 0:half], sin, ALU.mult))
                pool.tensor_tensor(z[:, :, 0:half], rope_tmp[:, 0, :, 0:half], rope_tmp[:, 1, :, 0:half], ALU.subtract)
                then(pool.tensor_tensor(z[:, :, half:ROT], rope_tmp[:, 0, :, half:ROT], rope_tmp[:, 1, :, half:ROT], ALU.add))
                pool.tensor_copy(z[:, 0:1, 0:1], z[:, 0:1, 0:1]).then_inc(roped, 1)

            for t in range(TILES):
                pool.wait_ge(sq_done, t + 1)
                inverse_rms(N1, t, 1, sum_sq[:, N1, t:t + 1], rstd_ready)
            pool.dma_start(rope[:, :, :], rope_table.rearrange("(t p) c -> p t c", p=P)).then_inc(tables_in, 16)
            pool.dma_start(bias8[:, :], pattern_bias).then_inc(tables_in, 16)
            pool.dma_start(attn_gain[:, :], attn_out_g[0:1, :].to_broadcast([P, WIDTH])).then_inc(tables_in, 16)
            for g, w in enumerate((w_rgate, w_igate)):
                for e in range(2):
                    pool.dma_start(gate_w[e * HEAD_DIM:(e + 1) * HEAD_DIM, g, :, e * HEAD_DIM:(e + 1) * HEAD_DIM],
                                   w[0].rearrange("(c e) k d -> e k c d", e=2)[e]).then_inc(gate_w_in, 16)
            for r in range(2 * TILES):
                rope_tile(r)
            pool.wait_ge(lru_sum_read, 1)
            inverse_rms(LRU, 0, TILES, lru_sq[:, :], lru_rstd)
            def attention_tile(t):
                pool.wait_ge(att_sq, t + 1)
                then(pool.tensor_tensor(att[:, 1, :], att[:, 0, :], attn_gain[:, :], ALU.mult))
                pool.tensor_copy(att[:, 1, 0:1], att[:, 1, 0:1]).then_inc(att_gained, 1)
                inverse_rms(ATT, t, 1, sum_sq[:, ATT, t:t + 1], att_rstd)

            def norm2_tile(t):
                pool.wait_ge(sq2_done, 2 * (t + 1))
                add_halves(N2, t)
                inverse_rms(N2, t, 1, sum_sq[:, N2, t:t + 1], rstd2_ready)

            attention_tile(0)
            attention_tile(1)
            attention_tile(2)
            norm2_tile(0)
            attention_tile(3)
            norm2_tile(1)
            norm2_tile(2)
            norm2_tile(3)
            for t in range(TILES):
                pool.wait_ge(sq3_done, TILES + t + 1)
                add_halves(FIN, t)
                inverse_rms(FIN, t, 1, sum_sq[:, FIN, t:t + 1], rstd3_ready)

        @block.tensor
        def _(pe):
            def three_passes(dst, a_hi, a_lo, b_hi, b_lo, first, last):
                pe.matmul(dst, a_hi, b_hi, start=first, stop=False)
                pe.matmul(dst, a_hi, b_lo, start=False, stop=False)
                return pe.matmul(dst, a_lo, b_hi, start=False, stop=last)

            def token_major(dst, act_hi, act_lo, kb, t, n, k, first, last):
                s = slot_of(n)
                return three_passes(dst, act_hi[:, kb, t * P:(t + 1) * P], act_lo[:, kb, t * P:(t + 1) * P],
                                    w_hi[s][:, k, :], w_lo[s][:, k, :], first, last)

            def channel_major(dst, kb, m, n, k, first, last):
                s = slot_of(n)
                return three_passes(dst, w_hi[s][:, k, m * P:(m + 1) * P], w_lo[s][:, k, m * P:(m + 1) * P],
                                    u_hi[:, kb, :], u_lo[:, kb, :], first, last)

            def turn_rows(src, pair, t, done):
                for kb in range(KB):
                    last = pe.transpose(ps[pair][:, kb * P:(kb + 1) * P], src[:, t % 2, kb * P:(kb + 1) * P], ident[:, :])
                last.then_inc(done, 1)

            def turn_qk(r):
                pe.wait_ge(roped, r + 1)
                if r >= 2:
                    pe.wait_ge(qk_evac, r - 1)
                for c in range(CB):
                    last = pe.transpose(bank(6 + r % 2)[:, c * P:(c + 1) * P], prob[:, r % 3, c * P:(c + 1) * P], ident[:, :])
                last.then_inc(qk_turned, 1)

            def gates(c):
                pe.wait_ge(conv_done, c + 1)
                if c == 0:
                    pe.wait_ge(gate_w_in, 64)
                else:
                    pe.wait_ge(sig_done, 2 * c)
                pe.matmul(bank(2), gate_w[:, 0, c, :], hidden[:, c, :], start=True, stop=True)
                pe.matmul(bank(3), gate_w[:, 1, c, :], hidden[:, c, :], start=True, stop=True).then_inc(gates_done, 1)

            def lru_sums():
                pe.wait_ge(y_sq_added, CB - 1)
                for t in range(TILES):
                    last = pe.matmul(bank(7)[:, t:t + 1], conv_in[:, 0, t * P:(t + 1) * P], ones[:, :], start=True, stop=True)
                last.then_inc(lru_sum_done, 1)

            def scores(i):
                t, h = divmod(i, HEADS)
                e, n = h % 2 * HEAD_DIM, (t + 1) * P
                if h == 0:
                    pe.wait_ge(qk_evac, TILES + t + 1)
                if i >= 2:
                    pe.wait_ge(max_done, i - 1)
                pe.matmul(bank(2 + i % 2, n), qT[e:e + HEAD_DIM, h // 2, t * P:(t + 1) * P],
                          kT[e:e + HEAD_DIM, h // 2, 0:n], start=True, stop=True).then_inc(scores_done, 1)

            def turn_probs(i):
                pe.wait_ge(exp_done, i + 1)
                for kt in range(i // HEADS + 1):
                    last = pe.transpose(bank(4 + i % 2)[:, kt * P:(kt + 1) * P], prob[:, i % 3, kt * P:(kt + 1) * P], ident[:, :])
                last.then_inc(prob_turned, 1)

            def weighted_values(i):
                t, h = divmod(i, HEADS)
                pe.wait_ge(odd_evac if i % 2 else even_evac, i // 2 + 1)
                if i == 0:
                    pe.wait_ge(qk_evac, 2 * TILES)
                    pe.wait_ge(in_evac, IN_STEPS - TILES + 1)
                if h == 0 and t:
                    pe.wait_ge(in_evac, IN_STEPS - TILES + t + 1)
                if h == 0 and t == 1:
                    pe.wait_ge(lru_sum_read, 1)
                if h == 0 and t >= 2:
                    pe.wait_ge(att_ready, t - 1)
                for kt in range(t + 1):
                    last = pe.matmul(bank(6 + t % 2)[:, h * HEAD_DIM:(h + 1) * HEAD_DIM],
                                     prob_t[:, i % 2, kt * P:(kt + 1) * P],
                                     values[:, kt, h * HEAD_DIM:(h + 1) * HEAD_DIM], start=(kt == 0), stop=(kt == t))
                last.then_inc(pv_done, 1)

            def turn_att(t):
                pe.wait_ge(att_gained, t + 1)
                for c in range(CB):
                    last = pe.transpose(bank(6 + t % 2)[:, c * P:(c + 1) * P], att[:, 1, c * P:(c + 1) * P], ident[:, :])
                last.then_inc(att_turned, 1)

            def attention_hook(k):
                if 1 <= k <= ITEMS:
                    scores(k - 1)
                if 3 <= k <= ITEMS + 2:
                    turn_probs(k - 3)
                if 4 <= k <= ITEMS + 3:
                    weighted_values(k - 4)
                if k >= 14 and (k - 14) % HEADS == 0 and (k - 14) // HEADS < TILES:
                    turn_att((k - 14) // HEADS)

            def turn_rows1(t):
                pe.wait_ge(row_normed, t + 1)
                if t >= 2:
                    pe.wait_ge(u_ready, t - 1)
                turn_rows(normed1, 1 + t % 2, t, rows_turned)

            pe.wait_ge(consts_ready, 1)
            turn_rows1(0)
            for panel, (what, _) in enumerate(IN_PANELS):
                for m in range(TILES):
                    s = TILES * panel + m
                    if s >= 2:
                        pe.wait_ge(in_evac, s - 1)
                    if panel == 0:
                        pe.wait_ge(u_ready, m + 1)
                    for kb in range(KB):
                        q, k = divmod(kb, UNIT_KB)
                        n = PANEL_UNITS * panel + q
                        if m == 0 and k == 0:
                            pe.wait_ge(lo_done, n + 1)
                        if what in ("xl", "gl"):
                            last = channel_major(bank(s % 2), kb, m, n, k, kb == 0, kb == KB - 1)
                        else:
                            last = token_major(bank(s % 2), u_hi, u_lo, kb, m, n, k, kb == 0, kb == KB - 1)
                        if kb == KB - 1:
                            last.then_inc(step_done, 1)
                        elif m == TILES - 1 and k == UNIT_KB - 1:
                            last.then_inc(unit_used, 1)
                        if k == 0:
                            continue
                        if what == "q" and q == 1 and m < TILES - 1:
                            turn_rows1(m + 1)
                        if what == "q" and m == 1 and q == 3:
                            pe.wait_ge(param_in, 96)
                            pe.transpose(bank(7)[:, 0:PARAM_ROWS], param_rows[:, :],
                                         ident[0:PARAM_ROWS, 0:PARAM_ROWS]).then_inc(params_turned, 1)
                        if what == "xl" and q == 0:
                            turn_qk(m)
                        if what == "xl" and q == 0 and m >= 2:
                            gates(m - 2)
                        if what == "xl" and q == 3 and m == 3:
                            gates(2)
                        if what == "gl" and q == 3 and m == 0:
                            gates(3)
                        if what == "k" and q == 2 and m >= 1:
                            turn_qk(TILES + m - 1)
                        if what == "v":
                            if m == 0 and q == 1:
                                turn_qk(2 * TILES - 1)
                            if m == 1 and q == 3:
                                lru_sums()
                            attention_hook(4 * m + q - LAG)
            for hf in range(2):
                for t in range(TILES):
                    r = TILES * hf + t
                    if r < 2:
                        pe.wait_ge(in_evac, IN_STEPS - 1 + r)
                    else:
                        pe.wait_ge(out_evac, r - 1)
                    if r == 0:
                        pe.wait_ge(lru_ready, CB)
                    for kb in range(CB):
                        q, k = divmod(kb, UNIT_KB)
                        n = IN_UNITS + 2 * hf + q
                        if t == 0 and k == 0:
                            pe.wait_ge(lo_done, n + 1)
                        last = token_major(bank(r % 2), lru_hi, lru_lo, kb, t, n, k, kb == 0, kb == CB - 1)
                        if kb == CB - 1:
                            last.then_inc(step_done, 1)
                        elif t == TILES - 1 and k == UNIT_KB - 1:
                            last.then_inc(unit_used, 1)
                        if k:
                            attention_hook(16 + 2 * r + q - LAG)
            for t in range(TILES):
                pe.wait_ge(att_ready, t + 1)
                for hf in range(2):
                    r = 8 + 2 * t + hf
                    pe.wait_ge(out_evac, r - 1)
                    for kb in range(CB):
                        q, k = divmod(kb, UNIT_KB)
                        n = IN_UNITS + 4 + 2 * hf + q
                        if t == 0 and k == 0:
                            pe.wait_ge(lo_done, n + 1)
                        last = token_major(bank(r % 2), att_hi, att_lo, kb, t, n, k, kb == 0, kb == CB - 1)
                        if kb == CB - 1:
                            last.then_inc(step_done, 1)
                        elif t == TILES - 1 and k == UNIT_KB - 1:
                            last.then_inc(unit_used, 1)
                        if k:
                            attention_hook(32 + 2 * (r - 8) + q - LAG)
                for turned in ([], [0], [1], [2, 3])[t]:
                    pe.wait_ge(row2_normed, turned + 1)
                    if turned >= 2:
                        pe.wait_ge(u2_ready, turned - 1)
                    turn_rows(normed, 1 + turned % 2, turned, rows2_turned)
            pe.wait_ge(u2_ready, TILES)
            with pe.Fori(0, GROUPS) as i:
                for j in range(4):
                    for m in range(TILES):
                        step = TILES * (j % 2) + m
                        pe.wait_ge(up_free if j < 2 else down_free, 8 * i + step + 1)
                        dst = bank((0 if j < 2 else BANKS) + step % BANKS)
                        for kb in range(KB):
                            q, k = divmod(kb, UNIT_KB)
                            n = MIX_UNITS + PANEL_UNITS * j + q
                            if m == 0 and k == 0:
                                pe.wait_ge(lo_done, GROUP_UNITS * i + n + 1)
                            if j < 2:
                                last = channel_major(dst, kb, m, n, k, kb == 0, kb == KB - 1)
                            else:
                                if j == 2 and m == 0:
                                    pe.wait_ge(f_ready, 8 * i + kb + 1)
                                last = token_major(dst, f_hi, f_lo, kb, m, n, k, kb == 0, kb == KB - 1)
                            if kb == KB - 1:
                                last.then_inc(up_done if j < 2 else down_done, 1)
                            elif m == TILES - 1 and k == UNIT_KB - 1:
                                last.then_inc(mlp_unit_used, 1)

        @block.scalar
        def _(act):
            act.dma_start(gain[:, :], norm1_g[0:1, :].to_broadcast([P, D_MODEL])).then_inc(gain1_in, 16)

            def split_hi(n):
                act.wait_ge(raw_in[n % RAW], 16 * (n // RAW + 1))
                wait_split_slot(act, n)
                act.activation(w_hi[slot_of(n)][:, :, :], raw[:, n % RAW, :, :], ACT.Copy).then_inc(hi_done, 1)

            def row_sum1(t):
                act.wait_ge(x_in[t], 16)
                if t:
                    act.wait_ge(sq_done, t)
                act.activation(gate_r[:, 0:2, :].rearrange("p a s -> p (a s)"), xs[:, t, :], ACT.Square,
                               accum_out=sum_sq[:, N1, t:t + 1]).then_inc(sq_done, 1)

            def u_hi_tile(t, turned, done):
                act.wait_ge(turned, t + 1)
                act.activation(u_hi[:, :, t * P:(t + 1) * P], ps[1 + t % 2][:, :].rearrange("p (k s) -> p k s", s=P),
                               ACT.Copy).then_inc(done, 1)

            def evacuate(s):
                panel, m = divmod(s, TILES)
                what = IN_PANELS[panel][0]
                act.wait_ge(step_done, s + 1)
                if what in ("q", "k"):
                    r = m if what == "q" else TILES + m
                    if r >= 3:
                        act.wait_ge(qk_turned, r - 2)
                    dst = prob[:, r % 3, :]
                elif what == "xl":
                    if m == 0:
                        act.wait_ge(consts_ready, 1)
                    dst = conv_in[:, m, CONV_WIDTH - 1:]
                elif what == "gl":
                    dst = gelu_g[:, m, :]
                else:
                    if m == 0:
                        act.wait_ge(root_arg, CB)
                    dst = values[:, m, :]
                act.activation(dst, bank(s % 2), ACT.Gelu_apprx_tanh if what == "gl" else ACT.Copy).then_inc(in_evac, 1)

            def sigmoids(c):
                act.wait_ge(gates_done, c + 1)
                if c == 0:
                    act.wait_ge(params_ready, 1)
                act.activation(gate_r[:, c, :], bank(2), ACT.Sigmoid, bias=params[:, 24 + c:25 + c]).then_inc(sig_done, 1)
                act.activation(gate_in[:, c, :], bank(3), ACT.Sigmoid, bias=params[:, 28 + c:29 + c]).then_inc(sig_done, 1)

            def decays(c):
                act.wait_ge(sig_done, 2 * c + 2)
                act.activation(decay_a[:, c, :], gate_r[:, c, :], ACT.Exp, scale=decay[:, 0, c:c + 1]).then_inc(a_done, 1)
                act.activation(gate_r[:, c, :], gate_r[:, c, :], ACT.Tanh, scale=decay[:, 1, c:c + 1]).then_inc(tanh_done, 1)

            def roots(c):
                act.wait_ge(root_arg, c + 1)
                act.activation(conv_in[:, c, 0:SEQ], conv_in[:, c, 0:SEQ], ACT.Sqrt).then_inc(root_done, 1)

            def lru_output(c):
                act.wait_ge(y_done, c + 1)
                act.activation(conv_in[:, c, 0:SEQ], hidden[:, c, :], ACT.Square).then_inc(y_sq_done, 1)

            def lru_output_hi(c):
                act.wait_ge(y_done, CB)
                act.activation(lru_hi[:, c, :], hidden[:, c, :], ACT.Copy, scale=params[:, 32 + c:33 + c]).then_inc(lru_hi_done, 1)

            def exponentials(i):
                n = (i // HEADS + 1) * P
                act.wait_ge(max_done, i + 1)
                act.activation(prob[:, i % 3, 0:n], prob[:, i % 3, 0:n], ACT.Exp, bias=neg_max[:, i:i + 1], scale=-1.0,
                               accum_out=denom[:, i:i + 1]).then_inc(exp_done, 1)

            def attention_hook(k):
                if 1 <= k <= ITEMS:
                    exponentials(k - 1)
                i = k - 3
                if 0 <= i < ITEMS and i % 2 == 0:
                    n = (i // HEADS + 1) * P
                    act.wait_ge(prob_turned, i + 1)
                    if i >= 2:
                        act.wait_ge(pv_done, i - 1)
                    act.activation(prob_t[:, 0, 0:n], bank(4, n), ACT.Copy).then_inc(even_evac, 1)
                if k >= 12 and (k - 12) % HEADS == 0 and (k - 12) // HEADS < TILES:
                    t = (k - 12) // HEADS
                    act.wait_ge(att_out, t + 1)
                    if t:
                        act.wait_ge(att_turned, t)
                    act.activation(att[:, 1, :], att[:, 0, :], ACT.Square, accum_out=sum_sq[:, ATT, t:t + 1]).then_inc(att_sq, 1)
                if k >= 15 and (k - 15) % HEADS == 0 and (k - 15) // HEADS < TILES:
                    t = (k - 15) // HEADS
                    act.wait_ge(att_turned, t + 1)
                    act.activation(att_hi[:, :, t * P:(t + 1) * P], bank(6 + t % 2).rearrange("p (c s) -> p c s", s=P),
                                   ACT.Copy).then_inc(att_hi_done, 1)

            def row_sum2(t, hf):
                act.wait_ge(out_evac, 8 + 2 * t + hf + 1)
                if t:
                    act.wait_ge(sq2_done, 2 * t + hf - 1)
                act.activation(prob_t[:, hf, :], xs[:, t, hf * COLS:(hf + 1) * COLS], ACT.Square,
                               accum_out=sum_sq[:, N2, TILES * hf + t:TILES * hf + t + 1]).then_inc(sq2_done, 1)

            row_sum1(0)
            split_hi(0)
            u_hi_tile(0, rows_turned, u_hi_done)
            split_hi(1)
            row_sum1(1)
            split_hi(2)
            split_hi(3)
            u_hi_tile(1, rows_turned, u_hi_done)
            row_sum1(2)
            row_sum1(3)
            for s in range(IN_STEPS):
                panel, m = divmod(s, TILES)
                n = PANEL_UNITS * (panel + 1)
                if m == 0 and s not in (12, 16):
                    split_hi(n)
                if m == 1 and s != 17:
                    split_hi(n + 1)
                if m == 3 and s != 19:
                    split_hi(n + 2)
                    if s != 15:
                        split_hi(n + 3)
                if s == 8:
                    sigmoids(3)
                if panel == 4:
                    for q in range(4):
                        if m == 1:
                            lru_output_hi(q)
                        if m == 0 and q == 2 or m == 2 and q == 0:
                            split_hi(n + m // 2)
                        attention_hook(4 * m + q - LAG)
                if s in (1, 2):
                    u_hi_tile(s + 1, rows_turned, u_hi_done)
                evacuate(s)
                if s == 2:
                    act.wait_ge(params_ready, 1)
                    act.activation(small[:, 0, :], params[:, 20:24], ACT.Abs).then_inc(exp_lam, 1)
                    act.wait_ge(exp_lam, 1)
                    act.activation(small[:, 1, :], small[:, 0, :], ACT.Exp, scale=-1.0).then_inc(exp_lam, 1)
                if 5 <= s <= 7:
                    sigmoids(s - 5)
                if s == 11:
                    act.wait_ge(decay_ready, 1)
                    for c in range(CB):
                        decays(c)
                if s == 12:
                    split_hi(n)
                if s == 13:
                    for c in range(CB):
                        roots(c)
                if s == 15:
                    split_hi(n + 3)
                if s in (14, 15):
                    lru_output(2 * s - 28)
                    lru_output(2 * s - 27)
            for r in range(8):
                attention_hook(16 + 2 * r - LAG)
                if r in (0, 1, 2, 3, 5, 6):
                    split_hi(IN_UNITS + 2 + min(r, 4) + (r == 6))
                attention_hook(17 + 2 * r - LAG)
            for r in range(8):
                attention_hook(32 + 2 * r - LAG)
                attention_hook(33 + 2 * r - LAG)
                if r == 1:
                    act.wait_ge(pv_done, ITEMS)
                if r % 2 and r < 7:
                    row_sum2(r // 2, 0)
                    row_sum2(r // 2, 1)
                if 2 <= r < 6:
                    split_hi(MIX_UNITS + r - 2)
                if r in (4, 6):
                    u_hi_tile(r // 2 - 2, rows2_turned, u2_hi_done)
            row_sum2(3, 0)
            row_sum2(3, 1)
            u_hi_tile(2, rows2_turned, u2_hi_done)
            u_hi_tile(3, rows2_turned, u2_hi_done)
            act.sem_inc(up_free, BANKS)

            def split_hi_mlp(i, j, q):
                n = MIX_UNITS + PANEL_UNITS * j + q
                act.wait_ge(raw_in[n % RAW], (16 * GROUP_UNITS // RAW) * i + 16 * (n // RAW + 1))
                wait_mlp_slot(act, i, j, q)
                act.activation(w_hi[slot_of(n)][:, :, :], raw[:, n % RAW, :, :], ACT.Copy).then_inc(hi_done, 1)

            def activate(i, u):
                act.wait_ge(up_done, 8 * i + u + 1)
                if not (isinstance(i, int) and 8 * i + u - 1 <= 0):
                    act.wait_ge(squared, 8 * i + u - 1)
                act.activation(relu[:, u % 2, :], bank(u % BANKS), ACT.Relu).then_inc(up_free, 1)
                act.wait_ge(up_free, 8 * i + u + 1 + BANKS)
                act.activation(f_hi[:, u, :], relu[:, u % 2, :], ACT.Square).then_inc(f_hi_done, 1)

            def to_up1(i, first):
                for m in range(TILES):
                    if first:
                        split_hi(MIX_UNITS + PANEL_UNITS + m)
                    else:
                        split_hi_mlp(i, 1, m)
                    activate(i, m)

            def to_down(i):
                for m in range(TILES):
                    split_hi_mlp(i, 2, m)
                    activate(i, TILES + m)
                for m in range(TILES):
                    split_hi_mlp(i, 3, m)

            to_up1(0, True)
            with act.Fori(0, GROUPS - 1) as i:
                to_down(i)
                for m in range(TILES):
                    split_hi_mlp(i + 1, 0, m)
                to_up1(i + 1, False)
            to_down(GROUPS - 1)
            for hf in range(2):
                for t in range(TILES):
                    act.wait_ge(down_free, BANKS + 8 * (GROUPS - 1) + TILES * hf + t + 1)
                    if TILES * hf + t >= 2:
                        act.wait_ge(sq3_done, TILES * hf + t - 1)
                    else:
                        act.wait_ge(sq2_done, 2 * TILES)
                    act.activation(prob_t[:, t % 2, :], xs[:, t, hf * COLS:(hf + 1) * COLS], ACT.Square,
                                   accum_out=sum_sq[:, FIN, TILES * hf + t:TILES * hf + t + 1]).then_inc(sq3_done, 1)

        @block.vector
        def _(dve):
            steps = [0]

            def then(ins):
                steps[0] += 1
                ins.then_inc(dve_step, 1)
                dve.wait_ge(dve_step, steps[0])

            def split_lo(n):
                dve.wait_ge(hi_done, n + 1)
                s = slot_of(n)
                dve.tensor_tensor(w_lo[s][:, :, :], raw[:, n % RAW, :, :], w_hi[s][:, :, :].bitcast(f32), ALU.subtract)\
                   .then_inc(lo_done, 1)

            def norm_rows(kind, t, dst, ready, done, free=None):
                dve.wait_ge(ready, t + 1)
                if free is not None and t >= 2:
                    dve.wait_ge(free, t - 1)
                dve.scalar_tensor_tensor(dst[:, t % 2, :], xs[:, t, :], rstd[:, kind, t:t + 1], gain[:, :],
                                         ALU.mult, ALU.mult).then_inc(done, 1)

            def u_lo_tile(t, hi, done):
                dve.wait_ge(hi, t + 1)
                dve.tensor_tensor(u_lo[:, :, t * P:(t + 1) * P], ps[1 + t % 2][:, :].rearrange("p (k s) -> p k s", s=P),
                                  u_hi[:, :, t * P:(t + 1) * P].bitcast(f32), ALU.subtract).then_inc(done, 1)

            def softplus():
                lam, e, z, z2, poly, rl = params[:, 20:24], small[:, 1, :], small[:, 2, :], small[:, 3, :], small[:, 4, :], small[:, 5, :]
                then(dve.tensor_scalar(z, e, 2.0, None, ALU.add))
                then(dve.reciprocal(z, z))
                then(dve.tensor_tensor(z, z, e, ALU.mult))
                then(dve.tensor_tensor(z2, z, z, ALU.mult))
                then(dve.tensor_scalar(poly, z2, 1.0 / 19, None, ALU.mult))
                for k in range(8, 0, -1):
                    then(dve.scalar_tensor_tensor(poly, poly, 1.0 / (2 * k + 1), z2, ALU.add, ALU.mult))
                then(dve.scalar_tensor_tensor(poly, poly, 1.0, z, ALU.add, ALU.mult))
                then(dve.tensor_scalar(rl, lam, -1.0, 0.0, ALU.mult, ALU.max))
                then(dve.scalar_tensor_tensor(poly, poly, 2.0, rl, ALU.mult, ALU.add))
                dve.tensor_scalar(decay[:, 0, :], poly, -8.0, None, ALU.mult)
                then(dve.tensor_scalar(decay[:, 1, :], poly, 8.0, None, ALU.mult))
                dve.tensor_scalar(small[:, 6, :], poly, 1.0, None, ALU.mult).then_inc(decay_ready, 1)

            def evacuate_qk(r):
                dve.wait_ge(qk_turned, r + 1)
                t = r % TILES
                dst = qT if r < TILES else kT
                dve.tensor_copy(dst[:, :, t * P:(t + 1) * P], bank(6 + r % 2).rearrange("p (c s) -> p c s", s=P)).then_inc(qk_evac, 1)

            def conv(c):
                dve.wait_ge(in_evac, TILES + c + 1)
                then(dve.tensor_scalar(hidden[:, c, :], conv_in[:, c, 0:SEQ], params[:, c:c + 1], params[:, 16 + c:17 + c],
                                       ALU.mult, ALU.add))
                for j in range(1, CONV_WIDTH):
                    ins = dve.scalar_tensor_tensor(hidden[:, c, :], conv_in[:, c, j:j + SEQ], params[:, j * CB + c:j * CB + c + 1],
                                                   hidden[:, c, :], ALU.mult, ALU.add)
                    if j < CONV_WIDTH - 1:
                        then(ins)
                ins.then_inc(conv_done, 1)

            def root_argument(c):
                dve.wait_ge(a_done, c + 1)
                dve.tensor_tensor(conv_in[:, c, 0:SEQ], decay_a[:, c, :], decay_a[:, c, :], ALU.mult).then_inc(a_sq_done, 1)
                dve.wait_ge(a_sq_done, c + 1)
                dve.wait_ge(tanh_done, c + 1)
                dve.scalar_tensor_tensor(conv_in[:, c, 0:SEQ], conv_in[:, c, 0:SEQ], 1.0, gate_r[:, c, :], ALU.add, ALU.mult)\
                   .then_inc(root_arg, 1)

            def gated_input(c):
                dve.wait_ge(sig_done, 2 * c + 2)
                dve.tensor_tensor(gate_in[:, c, :], gate_in[:, c, :], hidden[:, c, :], ALU.mult).then_inc(ix_done, 1)

            def recurrence(c):
                dve.wait_ge(root_done, c + 1)
                dve.wait_ge(ix_done, c + 1)
                then(dve.tensor_tensor(gate_in[:, c, :], gate_in[:, c, :], conv_in[:, c, 0:SEQ], ALU.mult))
                then(dve.tensor_tensor_scan(hidden[:, c, :], decay_a[:, c, :], gate_in[:, c, :], 0.0, ALU.mult, ALU.add))
                dve.tensor_tensor(hidden[:, c, :], hidden[:, c, :], gelu_g[:, c, :], ALU.mult).then_inc(y_done, 1)

            def add_squares(c):
                dve.wait_ge(y_sq_done, c + 1)
                if c > 1:
                    dve.wait_ge(y_sq_added, c - 1)
                dve.tensor_tensor(conv_in[:, 0, 0:SEQ], conv_in[:, 0, 0:SEQ], conv_in[:, c, 0:SEQ], ALU.add)\
                   .then_inc(y_sq_added, 1)

            def lru_output_lo(c):
                dve.wait_ge(lru_hi_done, c + 1)
                dve.scalar_tensor_tensor(lru_lo[:, c, :], hidden[:, c, :], params[:, 32 + c:33 + c],
                                         lru_hi[:, c, :].bitcast(f32), ALU.mult, ALU.subtract).then_inc(lru_ready, 1)

            def attention_hook(k):
                if k >= 12 and (k - 12) % HEADS == 0 and (k - 12) // HEADS < TILES:
                    t = (k - 12) // HEADS
                    dve.wait_ge(pv_done, HEADS * (t + 1))
                    if t:
                        dve.wait_ge(att_gained, t)
                    then(dve.reciprocal(inv_denom[:, HEADS * t:HEADS * (t + 1)], denom[:, HEADS * t:HEADS * (t + 1)]))
                    dve.tensor_tensor(att[:, 0, :].rearrange("p (h d) -> p h d", d=HEAD_DIM),
                                      bank(6 + t % 2).rearrange("p (h d) -> p h d", d=HEAD_DIM),
                                      inv_denom[:, HEADS * t:HEADS * (t + 1)].unsqueeze(2).to_broadcast([P, HEADS, HEAD_DIM]),
                                      ALU.mult).then_inc(att_out, 1)
                if 1 <= k <= ITEMS:
                    i = k - 1
                    t = i // HEADS
                    n = (t + 1) * P
                    dve.wait_ge(scores_done, i + 1)
                    if i == 0:
                        dve.wait_ge(tables_in, 48)
                    if i >= 3:
                        dve.wait_ge(prob_turned, i - 2)
                    dve.tensor_tensor_reduce(out=prob[:, i % 3, 0:n], in0=bank(2 + i % 2, n), in1=bias8[:, SEQ - n:SEQ],
                                             scale=-1.0 / HEAD_DIM ** 0.5, scalar=3e38, op0=ALU.add, op1=ALU.min,
                                             accum_out=neg_max[:, i:i + 1]).then_inc(max_done, 1)
                i = k - 3
                if 0 <= i < ITEMS and i % 2:
                    n = (i // HEADS + 1) * P
                    dve.wait_ge(prob_turned, i + 1)
                    if i >= 2:
                        dve.wait_ge(pv_done, i - 1)
                    dve.tensor_copy(prob_t[:, 1, 0:n], bank(5, n)).then_inc(odd_evac, 1)
                if k >= 15 and (k - 15) % HEADS == 0 and (k - 15) // HEADS < TILES:
                    t = (k - 15) // HEADS
                    dve.wait_ge(att_hi_done, t + 1)
                    dve.tensor_tensor(att_lo[:, :, t * P:(t + 1) * P], bank(6 + t % 2).rearrange("p (c s) -> p c s", s=P),
                                      att_hi[:, :, t * P:(t + 1) * P].bitcast(f32), ALU.subtract).then_inc(att_ready, 1)

            def add_output(r):
                if r < 8:
                    hf, t = divmod(r, TILES)
                    scale = rstd[:, LRU, t:t + 1]
                    if r == 0:
                        dve.wait_ge(lru_rstd, 1)
                else:
                    t, hf = divmod(r - 8, 2)
                    scale = rstd[:, ATT, t:t + 1]
                    dve.wait_ge(att_rstd, t + 1)
                dve.wait_ge(step_done, IN_STEPS + r + 1)
                part = xs[:, t, hf * COLS:(hf + 1) * COLS]
                dve.scalar_tensor_tensor(part, bank(r % 2), scale, part, ALU.mult, ALU.add).then_inc(out_evac, 1)

            dve.wait_ge(gain1_in, 16)
            norm_rows(N1, 0, normed1, rstd_ready, row_normed)
            split_lo(0)
            u_lo_tile(0, u_hi_done, u_ready)
            split_lo(1)
            norm_rows(N1, 1, normed1, rstd_ready, row_normed)
            split_lo(2)
            split_lo(3)
            u_lo_tile(1, u_hi_done, u_ready)
            norm_rows(N1, 2, normed1, rstd_ready, row_normed, rows_turned)
            norm_rows(N1, 3, normed1, rstd_ready, row_normed, rows_turned)
            for s in range(IN_STEPS):
                panel, m = divmod(s, TILES)
                n = PANEL_UNITS * (panel + 1)
                if s == 7:
                    evacuate_qk(3)
                if s in (7, 8):
                    conv(s - 5)
                if s in (1, 2):
                    u_lo_tile(s + 1, u_hi_done, u_ready)
                if m == 0 and s != 16:
                    split_lo(n)
                if m == 1 and s != 17:
                    split_lo(n + 1)
                if m == 3 and s != 19:
                    split_lo(n + 2)
                    split_lo(n + 3)
                if s == 1:
                    dve.wait_ge(params_turned, 1)
                    dve.tensor_copy(params[:, :], bank(7)[:, 0:PARAM_ROWS]).then_inc(params_ready, 1)
                if s == 3:
                    dve.wait_ge(exp_lam, 2)
                    softplus()
                if 4 <= s <= 6:
                    evacuate_qk(m)
                if s in (5, 6):
                    conv(s - 5)
                if panel == 2:
                    gated_input(m)
                if panel == 3 and m >= 1:
                    evacuate_qk(TILES + m - 1)
                if s == 12:
                    for c in range(CB):
                        root_argument(c)
                if s in (14, 15):
                    recurrence(2 * s - 28)
                    recurrence(2 * s - 27)
                if panel == 4:
                    if m == 0:
                        evacuate_qk(2 * TILES - 1)
                    for q in range(4):
                        if m == 0 and q == 2 or m == 2 and q == 0:
                            split_lo(n + m // 2)
                        if m == 2:
                            lru_output_lo(q)
                        attention_hook(4 * m + q - LAG)
                        if m == 0 and q:
                            add_squares(q)
                    if m == 1:
                        dve.wait_ge(lru_sum_done, 1)
                        dve.tensor_copy(lru_sq[:, :], bank(7)[:, 0:TILES]).then_inc(lru_sum_read, 1)
            for r in range(8):
                attention_hook(16 + 2 * r - LAG)
                if r in (0, 1, 2, 3, 5, 6):
                    split_lo(IN_UNITS + 2 + min(r, 4) + (r == 6))
                attention_hook(17 + 2 * r - LAG)
                add_output(r)
            for r in range(8):
                attention_hook(32 + 2 * r - LAG)
                attention_hook(33 + 2 * r - LAG)
                add_output(8 + r)
                if r in (2, 4, 6):
                    if r == 2:
                        dve.wait_ge(gain2_in, 16)
                    norm_rows(N2, r // 2 - 1, normed, rstd2_ready, row2_normed, rows2_turned)
                if 2 <= r < 6:
                    split_lo(MIX_UNITS + r - 2)
                if r in (4, 6):
                    u_lo_tile(r // 2 - 2, u2_hi_done, u2_ready)
            norm_rows(N2, 3, normed, rstd2_ready, row2_normed, rows2_turned)
            u_lo_tile(2, u2_hi_done, u2_ready)
            u_lo_tile(3, u2_hi_done, u2_ready)
            dve.sem_inc(down_free, BANKS)

            def split_lo_mlp(i, j, q):
                n = MIX_UNITS + PANEL_UNITS * j + q
                dve.wait_ge(hi_done, GROUP_UNITS * i + n + 1)
                s = slot_of(n)
                dve.tensor_tensor(w_lo[s][:, :, :], raw[:, n % RAW, :, :], w_hi[s][:, :, :].bitcast(f32), ALU.subtract)\
                   .then_inc(lo_done, 1)

            def square(i, u):
                dve.wait_ge(up_free, 8 * i + u + 1 + BANKS)
                dve.tensor_tensor(f_full[:, u % 2, :], relu[:, u % 2, :], relu[:, u % 2, :], ALU.mult).then_inc(squared, 1)
                dve.wait_ge(squared, 8 * i + u + 1)
                dve.wait_ge(f_hi_done, 8 * i + u + 1)
                dve.tensor_tensor(f_lo[:, u, :], f_full[:, u % 2, :], f_hi[:, u, :].bitcast(f32), ALU.subtract).then_inc(f_ready, 1)

            def add_down(i, d):
                hf, t = divmod(d, TILES)
                dve.wait_ge(down_done, 8 * i + d + 1)
                part = xs[:, t, hf * COLS:(hf + 1) * COLS]
                dve.tensor_tensor(part, bank(BANKS + d % BANKS), part, ALU.add).then_inc(down_free, 1)

            def to_up1(i, first):
                for m in range(TILES):
                    if first:
                        split_lo(MIX_UNITS + PANEL_UNITS + m)
                    else:
                        split_lo_mlp(i, 1, m)
                    square(i, m)

            def to_down(i):
                for m in range(TILES):
                    split_lo_mlp(i, 2, m)
                    square(i, TILES + m)
                for m in range(TILES):
                    split_lo_mlp(i, 3, m)
                    add_down(i, m)

            to_up1(0, True)
            with dve.Fori(0, GROUPS - 1) as i:
                to_down(i)
                for m in range(TILES):
                    split_lo_mlp(i + 1, 0, m)
                    add_down(i, TILES + m)
                to_up1(i + 1, False)
            to_down(GROUPS - 1)
            dve.wait_ge(final_gain_in, 16)
            for t in range(TILES):
                add_down(GROUPS - 1, TILES + t)
                dve.wait_ge(rstd3_ready, t + 1)
                if t >= 2:
                    dve.wait_ge(out_stored[t % 2], 16)
                dve.scalar_tensor_tensor(normed[:, t % 2, :], xs[:, t, :], rstd[:, FIN, t:t + 1], final_gain[:, :],
                                         ALU.mult, ALU.mult).then_inc(final_normed, 1)


_INS = ["x", "norm1_g", "w_in", "conv_w", "conv_b", "w_rgate", "b_rgate", "w_igate", "b_igate", "lru_lambda",
        "attn_out_g", "lru_out_g", "w_out", "norm2_g", "w_mlp_up", "w_mlp_down", "final_g"]


def kernel(**inputs):
    import numpy as np
    import concourse.bacc as bacc
    from concourse.bass_utils import run_bass_kernel_spmd as run

    back = np.arange(P)[:, None] + (SEQ - P) - np.arange(SEQ)[None, :]
    count = sum(((back >= 0) & (back <= w) & (back % d == 0)).astype(np.float64) for w, d in ((128, 1), (512, 4), (2048, 16)))
    bias8 = np.where(count > 0, np.log(np.maximum(count, 1.0)) * HEAD_DIM ** 0.5, MASKED).astype(np.float32)
    inv_freq = np.float32(500000.0) ** (-np.arange(0, ROT, 2, dtype=np.float32) / np.float32(ROT))
    angle = np.arange(SEQ, dtype=np.float32)[:, None] * inv_freq[None, :].astype(np.float32)
    cos, sin = np.cos(angle), np.sin(angle)
    rope = np.concatenate([cos, cos, sin, sin], axis=1).astype(np.float32)

    nc = bacc.Bacc("TRN2", target_bir_lowering=False, num_devices=1)
    arrays = {f"in_{n}_dram": np.ascontiguousarray(inputs[n]) for n in _INS}
    arrays["pattern_bias_dram"], arrays["rope_dram"] = bias8, rope
    args = [nc.dram_tensor(n, a.shape, mybir.dt.from_np(a.dtype), kind="ExternalInput").ap() for n, a in arrays.items()]
    args.append(nc.dram_tensor("out_0_dram", (1, SEQ, D_MODEL), mybir.dt.float32, kind="ExternalOutput").ap())
    layer_kernel(nc, *args)
    return run(nc, [arrays], core_ids=[0]).results[0]["out_0_dram"]
```
